# Optimizing a Trainium2 kernel written in Bass

```python
import math
import jax, jax.numpy as jnp
from jax import lax
import numpy as np

D_MODEL = 1024
BATCH = 1
SEQ = 256
DEPTH = 1

N_MIXERS = 3
N_HEADS = 16
HEAD_DIM = D_MODEL // N_HEADS
D_FF = 4 * D_MODEL
NORM_EPS = 1e-6
REL_BUCKETS = 32
REL_MAX_DIST = 128
MOBA_BLOCK = 256
MOBA_TOPK = 3
MOBA_Q_CHUNK = 16
A_IN_COLS = 3 * N_HEADS * HEAD_DIM
SWA_WINDOW = 128
SWA_BLOCK = 128
SWA_KV_HEADS = 2
SWA_GROUP = N_HEADS // SWA_KV_HEADS
B_IN_COLS = (N_HEADS + 2 * SWA_KV_HEADS) * HEAD_DIM
DSA_KV_RANK = D_MODEL // 4
DSA_IDX_HEADS = 8
DSA_IDX_DIM = 64
DSA_TOPK_MAX = 256
DSA_Q_CHUNK = 128
C_SPLITS = [N_HEADS * HEAD_DIM, DSA_KV_RANK, DSA_IDX_HEADS * DSA_IDX_DIM, DSA_IDX_DIM, DSA_IDX_HEADS]
C_IN_COLS = sum(C_SPLITS)
N_A = len(range(0, DEPTH, N_MIXERS))
N_B = len(range(1, DEPTH, N_MIXERS))
N_C = len(range(2, DEPTH, N_MIXERS))

kernel_name = "hybrid_moba_swa_dsa_trunk"

def rmsnorm(x, g):
    xf = x.astype(jnp.float32)
    y = xf * lax.rsqrt(jnp.mean(xf * xf, axis=-1, keepdims=True) + NORM_EPS)
    return (y * g.astype(jnp.float32)).astype(x.dtype)

def rel_bucket(dist):
    n = jnp.maximum(dist, 0)
    max_exact = REL_BUCKETS // 2
    nf = jnp.maximum(n, 1).astype(jnp.float32)
    large = max_exact + (jnp.log(nf / max_exact) / math.log(REL_MAX_DIST / max_exact)
                         * (REL_BUCKETS - max_exact)).astype(jnp.int32)
    large = jnp.minimum(large, REL_BUCKETS - 1)
    return jnp.where(n < max_exact, n, large)

def squared_relu_mlp(h, w_up, w_down):
    return jnp.square(jax.nn.relu(h @ w_up)) @ w_down

def moba_attention(h, w_in, w_out, rel_bias):
    B, S, _ = h.shape
    H, dh, BLK, QC = N_HEADS, HEAD_DIM, MOBA_BLOCK, MOBA_Q_CHUNK
    q, k, v = jnp.split(h @ w_in, 3, axis=-1)
    to_heads = lambda t: t.reshape(B, S, H, dh).transpose(0, 2, 1, 3)
    q, k, v = to_heads(q), to_heads(k), to_heads(v)
    nb = -(-S // BLK)
    pad = ((0, 0), (0, 0), (0, nb * BLK - S), (0, 0))
    k, v = jnp.pad(k, pad), jnp.pad(v, pad)
    kb = k.reshape(B, H, nb, BLK, dh)
    vb = v.reshape(B, H, nb, BLK, dh)
    k_mean = jnp.mean(kb, axis=3)
    n_sel = min(MOBA_TOPK, nb)
    scale = dh ** -0.5
    bias_hb = rel_bias.T
    b_idx = jnp.arange(B)[:, None, None, None]
    h_idx = jnp.arange(H)[None, :, None, None]
    blk_ids = jnp.arange(nb)
    j_in = jnp.arange(BLK)

    def chunk(start):
        qc = lax.dynamic_slice_in_dim(q, start, QC, axis=2)
        t = start + jnp.arange(QC)
        qb = start // BLK
        gate = jnp.einsum('bhqd,bhnd->bhqn', qc, k_mean).astype(jnp.float32)
        gate = jnp.where(blk_ids < qb, gate, -jnp.inf)
        _, sel = lax.top_k(gate, n_sel)
        valid = sel < qb
        k_sel = kb[b_idx, h_idx, sel]
        v_sel = vb[b_idx, h_idx, sel]
        s_past = jnp.einsum('bhqd,bhqnkd->bhqnk', qc, k_sel).astype(jnp.float32) * scale
        dist_past = t[:, None, None] - (sel[..., None] * BLK + j_in)
        s_past = s_past + bias_hb[h_idx[..., None], rel_bucket(dist_past)]
        s_past = jnp.where(valid[..., None], s_past, -jnp.inf).reshape(B, H, QC, n_sel * BLK)
        k_own = lax.dynamic_slice_in_dim(k, qb * BLK, BLK, axis=2)
        v_own = lax.dynamic_slice_in_dim(v, qb * BLK, BLK, axis=2)
        s_own = jnp.einsum('bhqd,bhkd->bhqk', qc, k_own).astype(jnp.float32) * scale
        dist_own = t[:, None] - (qb * BLK + j_in)[None, :]
        s_own = s_own + rel_bias[rel_bucket(dist_own)].transpose(2, 0, 1)
        s_own = jnp.where(dist_own >= 0, s_own, -jnp.inf)
        p = jax.nn.softmax(jnp.concatenate([s_past, s_own], axis=-1), axis=-1)
        p_past = p[..., :n_sel * BLK].reshape(B, H, QC, n_sel, BLK).astype(v.dtype)
        p_own = p[..., n_sel * BLK:].astype(v.dtype)
        return (jnp.einsum('bhqnk,bhqnkd->bhqd', p_past, v_sel)
                + jnp.einsum('bhqk,bhkd->bhqd', p_own, v_own))

    o = lax.map(chunk, jnp.arange(S // QC) * QC)
    o = o.transpose(1, 0, 3, 2, 4).reshape(B, S, H * dh)
    return o @ w_out

def swa_sink_attention(h, w_in, sinks, w_out, rel_bias):
    B, S, _ = h.shape
    HKV, G, dh, BLK = SWA_KV_HEADS, SWA_GROUP, HEAD_DIM, SWA_BLOCK
    proj = h @ w_in
    nq = N_HEADS * dh
    q = proj[..., :nq].reshape(B, S, HKV, G, dh)
    k = proj[..., nq:nq + HKV * dh].reshape(B, S, HKV, dh)
    v = proj[..., nq + HKV * dh:].reshape(B, S, HKV, dh)
    nb = S // BLK
    qb = q.reshape(B, nb, BLK, HKV, G, dh)
    pad = ((0, 0), (BLK, 0), (0, 0), (0, 0))
    kp = jnp.pad(k, pad).reshape(B, nb + 1, BLK, HKV, dh)
    vp = jnp.pad(v, pad).reshape(B, nb + 1, BLK, HKV, dh)
    k_band = jnp.concatenate([kp[:, :-1], kp[:, 1:]], axis=2)
    v_band = jnp.concatenate([vp[:, :-1], vp[:, 1:]], axis=2)
    s = jnp.einsum('bnqkgd,bnskd->bnkgqs', qb, k_band).astype(jnp.float32) * dh ** -0.5
    dist = BLK + jnp.arange(BLK)[:, None] - jnp.arange(2 * BLK)[None, :]
    key_pos = jnp.arange(nb)[:, None] * BLK - BLK + jnp.arange(2 * BLK)[None, :]
    mask = ((dist >= 0) & (dist < SWA_WINDOW))[None] & (key_pos >= 0)[:, None, :]
    bias = rel_bias[rel_bucket(dist)].transpose(2, 0, 1).reshape(HKV, G, BLK, 2 * BLK)
    s = jnp.where(mask[None, :, None, None], s + bias, -jnp.inf)
    sink = jnp.broadcast_to(sinks.astype(jnp.float32).reshape(HKV, G)[None, None, :, :, None, None],
                            s.shape[:-1] + (1,))
    p = jax.nn.softmax(jnp.concatenate([s, sink], axis=-1), axis=-1)[..., :-1]
    o = jnp.einsum('bnkgqs,bnskd->bnqkgd', p.astype(v.dtype), v_band)
    return o.reshape(B, S, N_HEADS * dh) @ w_out

def dsa_attention(h, w_in, kv_norm, w_uk, w_uv, w_out, rel_bias):
    B, S, _ = h.shape
    H, dh, HI, dI, QC = N_HEADS, HEAD_DIM, DSA_IDX_HEADS, DSA_IDX_DIM, DSA_Q_CHUNK
    q, c_kv, q_idx, k_idx, w_idx = jnp.split(h @ w_in, list(np.cumsum(C_SPLITS)[:-1]), axis=-1)
    q = q.reshape(B, S, H, dh)
    c = rmsnorm(c_kv, kv_norm)
    q_lat = jnp.einsum('bthd,rhd->bthr', q, w_uk) * dh ** -0.5
    q_idx = q_idx.reshape(B, S, HI, dI)
    w_idx = w_idx * HI ** -0.5
    top_k = min(DSA_TOPK_MAX, S // 4)
    key_pos = jnp.arange(S)
    b_idx = jnp.arange(B)[:, None, None]

    def chunk(start):
        t = start + jnp.arange(QC)
        qi = lax.dynamic_slice_in_dim(q_idx, start, QC, axis=1)
        wi = lax.dynamic_slice_in_dim(w_idx, start, QC, axis=1)
        rel = jax.nn.relu(jnp.einsum('bqhd,bsd->bqhs', qi, k_idx).astype(jnp.float32) * dI ** -0.5)
        score = jnp.einsum('bqh,bqhs->bqs', wi.astype(jnp.float32), rel)
        score = jnp.where(key_pos[None, None, :] <= t[None, :, None], score, -jnp.inf)
        _, sel = lax.top_k(score, top_k)
        valid = sel <= t[None, :, None]
        c_sel = c[b_idx, sel]
        ql = lax.dynamic_slice_in_dim(q_lat, start, QC, axis=1)
        s = jnp.einsum('bqhr,bqkr->bhqk', ql, c_sel).astype(jnp.float32)
        s = s + rel_bias[rel_bucket(t[None, :, None] - sel)].transpose(0, 3, 1, 2)
        s = jnp.where(valid[:, None], s, -jnp.inf)
        p = jax.nn.softmax(s, axis=-1).astype(c.dtype)
        o_lat = jnp.einsum('bhqk,bqkr->bqhr', p, c_sel)
        return jnp.einsum('bqhr,rhd->bqhd', o_lat, w_uv)

    o = lax.map(chunk, jnp.arange(S // QC) * QC)
    o = o.transpose(1, 0, 2, 3, 4).reshape(B, S, H * dh)
    return o @ w_out

def setup_inputs(seed: int = 0) -> dict:
    key = jax.random.key(seed)
    ks = jax.random.split(key, 20)
    nrm = lambda k, shape, fan_in: jax.random.normal(k, shape, jnp.float32) * fan_in ** -0.5
    gain = lambda k, shape: 1.0 + 0.02 * jax.random.normal(k, shape, jnp.float32)
    D, HD = D_MODEL, N_HEADS * HEAD_DIM
    return {
        "x": jax.random.normal(ks[0], (BATCH, SEQ, D), jnp.float32),
        "rel_bias": 0.5 * jax.random.normal(ks[1], (REL_BUCKETS, N_HEADS), jnp.float32),
        "norm_mix": gain(ks[2], (DEPTH, D)),
        "norm_mlp": gain(ks[3], (DEPTH, D)),
        "mlp_up": nrm(ks[4], (DEPTH, D, D_FF), D),
        "mlp_down": nrm(ks[5], (DEPTH, D_FF, D), D_FF),
        "a_w_in": nrm(ks[6], (N_A, D, A_IN_COLS), D),
        "a_w_out": nrm(ks[7], (N_A, HD, D), HD),
        "b_w_in": nrm(ks[8], (N_B, D, B_IN_COLS), D),
        "b_sinks": 0.5 * jax.random.normal(ks[9], (N_B, N_HEADS), jnp.float32),
        "b_w_out": nrm(ks[10], (N_B, HD, D), HD),
        "c_w_in": nrm(ks[11], (N_C, D, C_IN_COLS), D),
        "c_kv_norm": gain(ks[12], (N_C, DSA_KV_RANK)),
        "c_w_uk": nrm(ks[13], (N_C, DSA_KV_RANK, N_HEADS, HEAD_DIM), DSA_KV_RANK),
        "c_w_uv": nrm(ks[14], (N_C, DSA_KV_RANK, N_HEADS, HEAD_DIM), DSA_KV_RANK),
        "c_w_out": nrm(ks[15], (N_C, HD, D), HD),
        "final_norm": gain(ks[16], (D,)),
    }

def reference(x, rel_bias, norm_mix, norm_mlp, mlp_up, mlp_down, a_w_in, a_w_out,
              b_w_in, b_sinks, b_w_out, c_w_in, c_kv_norm, c_w_uk, c_w_uv, c_w_out, final_norm):
    h = x
    for i in range(DEPTH):
        kind, j = i % N_MIXERS, i // N_MIXERS
        y = rmsnorm(h, norm_mix[i])
        if kind == 0:
            y = moba_attention(y, a_w_in[j], a_w_out[j], rel_bias)
        elif kind == 1:
            y = swa_sink_attention(y, b_w_in[j], b_sinks[j], b_w_out[j], rel_bias)
        else:
            y = dsa_attention(y, c_w_in[j], c_kv_norm[j], c_w_uk[j], c_w_uv[j], c_w_out[j], rel_bias)
        h = h + y
        h = h + squared_relu_mlp(rmsnorm(h, norm_mlp[i]), mlp_up[i], mlp_down[i])
    return rmsnorm(h, final_norm)


_drawn_inputs = setup_inputs


def setup_inputs(seed=0):
    import zlib

    import numpy as np

    out = dict(_drawn_inputs(seed))
    spreads = {}
    factors = {'norm_mix': 7.759, 'norm_mlp': 10.056, 'final_norm': 8.176}
    for name, (base, spread) in spreads.items():
        noise = np.random.default_rng([zlib.crc32(name.encode()), seed]).standard_normal(out[name].shape)
        drawn = base * np.exp(spread * noise) if base else spread * noise
        out[name] = __import__('jax').numpy.asarray(drawn.astype(out[name].dtype))
    for name, factor in factors.items():
        out[name] = (out[name] * factor).astype(out[name].dtype)
    return out
```

```python
from contextlib import ExitStack

import numpy as np

import concourse.bass as bass
from concourse import mybir

F32 = mybir.dt.float32
F32R = mybir.dt.float32r
ALU = mybir.AluOpType
ACT = mybir.ActivationFunctionType

P = 128
D = 1024
T = 256
TB = T // P
KB = D // P
HEADS = 16
DH = D // HEADS
PAIRS = HEADS // 2
F = 4 * D
CW = 256
CHUNKS_IN = D // CW
CHUNKS_OUT = D // CW
CHUNKS_UP = F // CW
CE = D * CW // P
HALF = CE // 2
SLOTS = 4
OUT0 = 3 * CHUNKS_IN
MLP0 = OUT0 + CHUNKS_OUT
UNITS = 6
BUCKETS = 32
MAX_DIST = 128
BV = P + T
EPS = 1e-6
MASKED = 3.0e38
SCALE = DH ** -0.5
HI, LO = 0, 1


def shape_constants():
    dist = T - 1 - np.arange(BV)
    n = np.maximum(dist, 0)
    exact = BUCKETS // 2
    large = exact + (np.log(np.maximum(n, 1) / exact) / np.log(MAX_DIST / exact) * (BUCKETS - exact)).astype(np.int64)
    bucket = np.where(n < exact, n, np.minimum(large, BUCKETS - 1))
    onehot = (np.arange(BUCKETS)[:, None] == bucket[None, :]) & (dist >= 0)[None, :]
    fill = np.broadcast_to(np.where(dist < 0, MASKED, 0.0), (HEADS, BV))
    return {
        "identity": np.eye(P, dtype=np.float32),
        "bucket_onehot": onehot.astype(np.float32),
        "causal_fill": np.ascontiguousarray(fill, dtype=np.float32),
    }


def build(nc, x, rel_bias, norm_mix, norm_mlp, mlp_up, mlp_down, w_in, w_out, final_norm,
          identity, bucket_onehot, causal_fill, out):
    x_rows = x[0].rearrange("(b p) d -> b p d", p=P)
    out_rows = out[0].rearrange("(b p) d -> b p d", p=P)
    w_in_v = w_in[0].rearrange("(k p) n -> p k n", p=P)
    w_out_v = w_out[0].rearrange("(k p) n -> p k n", p=P)
    up_v = mlp_up[0].rearrange("(k p) n -> p k n", p=P)
    down_v = mlp_down[0].rearrange("(k p) n -> p k n", p=P)
    bias_dram = nc.dram_tensor("bias_by_distance", [HEADS, BV], F32, kind="Internal").ap()

    with ExitStack() as ctx:
        def sb(name, shape, dt=F32):
            return ctx.enter_context(nc.sbuf_tensor(name, shape, dt))

        def sem(name):
            return ctx.enter_context(nc.semaphore(name))

        h_sb = sb("h_sb", [P, TB, D])
        y_sb = sb("y_sb", [P, TB, D])
        yT = sb("yT", [P, KB, 2, T], F32R)
        raw = sb("raw", [P, SLOTS, CE])
        w_hi = sb("w_hi", [P, SLOTS, CE], F32R)
        w_lo = sb("w_lo", [P, SLOTS, CE], F32R)
        qT = sb("qT", [P, 2, T])
        kT = sb("kT", [P, 2, T])
        v_sb = sb("v_sb", [P, TB, D])
        bias_sb = sb("bias_sb", [P, 4, T])
        probs = sb("probs", [P, 4, 3 * P])
        pT = sb("pT", [P, 4, 3 * P])
        o_sb = sb("o_sb", [P, 2, TB, P])
        oT = sb("oT", [P, PAIRS, 2, T], F32R)
        negmax = sb("negmax", [P, 2, 4])
        rowsum = sb("rowsum", [P, 2, 4])
        rinv = sb("rinv", [P, 2, 4])
        part = sb("part", [P, 2, T])
        z_sb = sb("z_sb", [P, 2, T])
        s_sb = sb("s_sb", [P, 2, T])
        hT = sb("hT", [P, 2, 2, 2, T], F32R)
        gain = sb("gain", [P, D])
        ident = sb("ident", [P, P])
        rel_sb = sb("rel_sb", [BUCKETS, HEADS])
        onehot_sb = sb("onehot_sb", [BUCKETS, BV])
        fill_sb = sb("fill_sb", [HEADS, BV])
        bv_sb = sb("bv_sb", [HEADS, BV])
        stat = sb("stat", [P, 6, 4])

        bank = [ctx.enter_context(nc.psum_tensor(f"bank{i}", [P, 512], F32)) for i in range(8)]
        UNIT = [0, 1]
        SCORE = [2, 3, 4, 5]
        PV, OTB = 6, 7
        ACC = [[0, 1], [2, 3]]
        UP = [4, 5]
        NORM = [[4, 5], [6, 7]]

        raw_full = [sem(f"raw_full{i}") for i in range(SLOTS)]
        x_loaded = [sem(f"x_loaded{i}") for i in range(TB)]
        ident_loaded, tables_loaded = sem("ident_loaded"), sem("tables_loaded")
        gain_loaded, bias_loaded = sem("gain_loaded"), sem("bias_loaded")
        bias_summed, bias_vec, bias_stored = sem("bias_summed"), sem("bias_vec"), sem("bias_stored")
        raw_free, scores_seen = sem("raw_free"), sem("scores_seen")
        hi_done, lo_done = sem("hi_done"), sem("lo_done")
        ss_done, var_done, sd_done = sem("ss_done"), sem("var_done"), sem("sd_done")
        rstd_done, y_done = sem("rstd_done"), sem("y_done")
        yt_done, yhi_done, ylo_done = sem("yt_done"), sem("yhi_done"), sem("ylo_done")
        unit_done, v_ready, part_done, qk_ready = sem("unit_done"), sem("v_ready"), sem("part_done"), sem("qk_ready")
        scores_done, biased, exp_done = sem("scores_done"), sem("biased"), sem("exp_done")
        pt_done, pt_ready = sem("pt_done"), sem("pt_ready")
        rinv_done, pv_done, o_ready = sem("rinv_done"), sem("pv_done"), sem("o_ready")
        ot_done, othi_done, ot_ready = sem("ot_done"), sem("othi_done"), sem("ot_ready")
        mix_done, wout_used, h_done = sem("mix_done"), sem("wout_used"), sem("h_done")
        up_done, upart_done, z_done = sem("up_done"), sem("upart_done"), sem("z_done")
        s_done, hhi_done, hT_ready = sem("s_done"), sem("hhi_done"), sem("hT_ready")
        down_done, mlp_done, h2_done = sem("down_done"), sem("mlp_done"), sem("h2_done")
        out_ready, stored = sem("out_ready"), sem("stored")

        block = ctx.enter_context(nc.Block())

        def cols(slot_tensor, slot):
            return slot_tensor[:, slot, :].rearrange("p (k n) -> p k n", k=KB)

        def rows(slot_tensor, slot):
            return slot_tensor[:, slot, :].rearrange("p (k n) -> p k n", k=2)

        @block.sync
        def _(sp):
            def load(slot, src, split):
                if split is not None:
                    sp.wait_ge(lo_done, split)
                    sp.sem_inc(raw_free, 1)
                n = CE // src.shape[1]
                nc.sync.dma_start(raw[:, slot, :].rearrange("p (k n) -> p k n", n=n), src
                                  ).then_inc(raw_full[slot], 16)

            def triple(c, first):
                for slot, base in enumerate((2 * D, 0, D)):
                    load(slot, w_in_v[:, :, bass.ds(c * CW + base, CW)],
                         None if first else 6 * c - 4 + 2 * slot)

            for tb in range(TB):
                nc.sync.dma_start(h_sb[:, tb, :], x_rows[tb]).then_inc(x_loaded[tb], 16)
            triple(0, True)
            load(3, w_out_v[:, 6:8, :], None)
            with sp.Fori(1, CHUNKS_IN) as c:
                triple(c, False)
            for q in range(3):
                load(q, w_out_v[:, 2 * q:2 * q + 2, :], 2 * (OUT0 + q - 3 + 1))
            with sp.Fori(0, CHUNKS_UP // 2) as i:
                for r in range(2):
                    load(2 * r, up_v[:, :, bass.ds(i * 2 * CW + r * CW, CW)], 8 * i + 26 + 4 * r)
                    load(2 * r + 1, down_v[:, bass.ds(i * 4 + 2 * r, 2), :], 8 * i + 28 + 4 * r)
            for tb in range(TB):
                sp.wait_ge(out_ready, tb + 1)
                nc.sync.dma_start(out_rows[tb], y_sb[:, tb, :]).then_inc(stored, 16)
            sp.wait_ge(stored, 16 * TB)
            sp.wait_ge(bias_stored, 16)

        @block.gpsimd
        def _(pool):
            nc.gpsimd.dma_start(gain[:], norm_mix.partition_broadcast(P).rearrange("p a d -> p (a d)")
                                ).then_inc(gain_loaded, 16)
            nc.gpsimd.dma_start(ident[:], identity).then_inc(ident_loaded, 16)
            nc.gpsimd.dma_start(rel_sb[:], rel_bias).then_inc(tables_loaded, 16)
            nc.gpsimd.dma_start(onehot_sb[:], bucket_onehot).then_inc(tables_loaded, 16)
            nc.gpsimd.dma_start(fill_sb[:], causal_fill).then_inc(tables_loaded, 16)
            pool.wait_ge(bias_vec, 1)
            nc.gpsimd.dma_start(bias_dram, bv_sb[:]).then_inc(bias_stored, 16)
            pool.wait_ge(bias_stored, 16)

            def tiles(a):
                src = bass.AP(tensor=bias_dram.tensor, offset=bias_dram.offset + a * (4 * BV),
                              ap=[[1, P], [BV, 4], [1, T]])
                nc.gpsimd.dma_start(bias_sb[:], src).then_inc(bias_loaded, 16)

            tiles(0)
            pool.wait_ge(y_done, TB)
            nc.gpsimd.dma_start(gain[:], norm_mlp.partition_broadcast(P).rearrange("p a d -> p (a d)")
                                ).then_inc(gain_loaded, 16)
            with pool.Fori(1, CHUNKS_IN) as a:
                pool.wait_ge(biased, 4 * a)
                tiles(a)
            pool.wait_ge(y_done, 2 * TB)
            nc.gpsimd.dma_start(gain[:], final_norm.partition_broadcast(P)).then_inc(gain_loaded, 16)

        @block.tensor
        def _(pe):
            mm = nc.tensor.matmul

            def transposes(norm, tb):
                pe.wait_ge(y_done, norm * TB + tb + 1)
                if norm == 0 and tb == 0:
                    pe.wait_ge(ident_loaded, 16)
                for b in range(2):
                    for k in range(4):
                        last = nc.tensor.transpose(bank[NORM[tb][b]][:, k * P:(k + 1) * P],
                                                   y_sb[:, tb, (4 * b + k) * P:(4 * b + k + 1) * P], ident[:])
                    last.then_inc(yt_done, 1)

            def v_unit(c, tb, first):
                pe.wait_ge(lo_done, 6 * c + 2)
                if not first:
                    pe.wait_ge(qk_ready, 4 * c - 1 + tb)
                wh, wl = cols(w_hi, 0), cols(w_lo, 0)
                acc = bank[UNIT[tb]][:, 0:CW]
                tok = slice(tb * P, (tb + 1) * P)
                for k in range(KB):
                    mm(acc, yT[:, k, HI, tok], wh[:, k, :], start=(k == 0), stop=False)
                    mm(acc, yT[:, k, HI, tok], wl[:, k, :], start=False, stop=False)
                    last = mm(acc, yT[:, k, LO, tok], wh[:, k, :], start=False, stop=(k == KB - 1))
                last.then_inc(unit_done, 1)

            def qk_unit(c, u):
                slot = u // 2
                pe.wait_ge(lo_done, 6 * c + 2 * slot + 2)
                if u < 4:
                    pe.wait_ge(v_ready, 2 * c + u - 1)
                else:
                    pe.wait_ge(qk_ready, 4 * c + u - 3)
                feature_unit(bank[UNIT[u % 2]], slot, u % 2).then_inc(unit_done, 1)

            def feature_unit(dst, slot, i):
                wh, wl = cols(w_hi, slot), cols(w_lo, slot)
                own = slice(i * P, (i + 1) * P)
                for k in range(KB):
                    mm(dst[:], wh[:, k, own], yT[:, k, :, :], start=(k == 0), stop=False, skip_group_check=True)
                    last = mm(dst[:, 0:T], wl[:, k, own], yT[:, k, HI, :], start=False, stop=(k == KB - 1),
                              skip_group_check=True)
                return last

            def scores(a, p):
                pe.wait_ge(qk_ready, 4 * a + 3 + p)
                for h in range(2):
                    dst = bank[SCORE[2 * p + h]]
                    dims = slice(h * DH, (h + 1) * DH)
                    mm(dst[:, 0:P], qT[dims, p, P:T], kT[dims, p, 0:P], start=True, stop=True)
                    mm(dst[:, P:3 * P], qT[dims, p, 0:P], kT[dims, p, :], start=True, stop=True
                       ).then_inc(scores_done, 1)

            def probs_T(a, p):
                for h in range(2):
                    pe.wait_ge(exp_done, 4 * a + 2 * p + h + 1)
                    for b in range(3):
                        last = nc.tensor.transpose(bank[SCORE[2 * p + h]][:, b * P:(b + 1) * P],
                                                   probs[:, 2 * p + h, b * P:(b + 1) * P], ident[:])
                    last.then_inc(pt_done, 1)

            def values(a, p, first):
                if p == 1:
                    pe.wait_ge(o_ready, 2 * a + 1)
                for h in range(2):
                    s = 2 * p + h
                    pe.wait_ge(pt_ready, 4 * a + s + 1)
                    vcol = bass.ds(a * (4 * DH) + s * DH, DH)
                    o0 = bank[PV][:, h * DH:(h + 1) * DH]
                    o1 = bank[PV][:, P + h * DH:P + (h + 1) * DH]
                    mm(o0, pT[:, s, 0:P], v_sb[:, 0, vcol], start=True, stop=True)
                    mm(o1, pT[:, s, P:2 * P], v_sb[:, 0, vcol], start=True, stop=False)
                    last = mm(o1, pT[:, s, 2 * P:3 * P], v_sb[:, 1, vcol], start=False, stop=True)
                last.then_inc(pv_done, 1)

            def out_T(a, p):
                pe.wait_ge(o_ready, 2 * a + p + 1)
                if p == 1:
                    pe.wait_ge(ot_ready, 2 * a + 1)
                for tb in range(TB):
                    last = nc.tensor.transpose(bank[OTB][:, (1 - tb) * P:(2 - tb) * P], o_sb[:, p, tb, :], ident[:])
                last.then_inc(ot_done, 1)

            def accumulate(lhs, slot, r, tb, start, stop):
                wh, wl = rows(w_hi, slot), rows(w_lo, slot)
                for l, w, first in ((HI, wh, start), (HI, wl, False), (LO, wh, False)):
                    for c in range(2):
                        last = mm(bank[ACC[tb][c]][:], lhs(l), w[:, r, c * 512:(c + 1) * 512],
                                  start=first, stop=(stop and l == LO))
                return last

            def mix(tb, k):
                q = k // 2
                pe.wait_ge(lo_done, 2 * (OUT0 + q) + 2)
                pe.wait_ge(ot_ready, k + 1)
                last = accumulate(lambda l: oT[:, k, l, tb * P:(tb + 1) * P], q, k % 2, tb, k == 0, k == PAIRS - 1)
                if tb == 1 and k % 2:
                    last.then_inc(wout_used, 1)
                elif k == PAIRS - 1:
                    last.then_inc(mix_done, 1)

            def up(f, par, i):
                pe.wait_ge(lo_done, 4 * f + 2 * MLP0 + 2)
                feature_unit(bank[UP[i]], 2 * par, i).then_inc(up_done, 1)

            def down(f, par, tb, start=False, stop=False):
                if tb == 0:
                    pe.wait_ge(lo_done, 4 * f + 2 * MLP0 + 4)
                    pe.wait_ge(hT_ready, 2 * f + 2)
                for i in range(2):
                    last = accumulate(lambda l: hT[:, par, i, l, tb * P:(tb + 1) * P], 2 * par + 1, i, tb,
                                      start and i == 0, stop and i == 1)
                return last

            def step(f, par, start=False):
                for i in range(2):
                    pe.wait_ge(z_done, 2 * f + i + 1)
                    up(f + 1, 1 - par, i)
                down(f, par, 0, start)
                down(f, par, 1, start).then_inc(down_done, 1)

            pe.wait_ge(tables_loaded, 48)
            mm(bank[0][0:HEADS, 0:BV], rel_sb[:], onehot_sb[:], start=True, stop=True).then_inc(bias_summed, 1)
            for tb in range(TB):
                transposes(0, tb)
            pe.wait_ge(bias_vec, 1)
            pe.wait_ge(ylo_done, 2)
            v_unit(0, 0, True)
            pe.wait_ge(ylo_done, 4)
            v_unit(0, 1, True)
            for u in range(2, UNITS):
                qk_unit(0, u)
            with pe.Fori(1, CHUNKS_IN) as c:
                scores(c - 1, 0)
                v_unit(c, 0, False)
                scores(c - 1, 1)
                v_unit(c, 1, False)
                probs_T(c - 1, 0)
                qk_unit(c, 2)
                values(c - 1, 0, False)
                probs_T(c - 1, 1)
                qk_unit(c, 3)
                values(c - 1, 1, False)
                out_T(c - 1, 0)
                qk_unit(c, 4)
                out_T(c - 1, 1)
                qk_unit(c, 5)
            a = CHUNKS_IN - 1
            scores(a, 0)
            scores(a, 1)
            for k in range(3):
                mix(0, k)
            probs_T(a, 0)
            probs_T(a, 1)
            for k in range(3, 5):
                mix(0, k)
            values(a, 0, False)
            mix(0, 5)
            values(a, 1, False)
            out_T(a, 0)
            mix(1, 0)
            out_T(a, 1)
            mix(1, 1)
            mix(0, 6)
            mix(0, 7)
            for k in range(2, PAIRS):
                mix(1, k)
            for tb in range(TB):
                transposes(1, tb)
            pe.wait_ge(ylo_done, 8)
            up(0, 0, 0)
            up(0, 0, 1)
            step(0, 0, True)
            step(1, 1)
            with pe.Fori(2, CHUNKS_UP - 2, 2) as f:
                step(f, 0)
                step(f + 1, 1)
            f = CHUNKS_UP - 2
            for i in range(2):
                pe.wait_ge(z_done, 2 * f + i + 1)
                up(f + 1, 1, i)
            down(f, 0, 0)
            down(f + 1, 1, 0, stop=True).then_inc(mlp_done, 1)
            down(f, 0, 1)
            down(f + 1, 1, 1, stop=True).then_inc(mlp_done, 1)

        @block.scalar
        def _(act):
            def hi(slot, half, count, full, used=None):
                act.wait_ge(raw_full[slot], full)
                if used is not None:
                    act.wait_ge(used[0], used[1])
                part_of = slice(half * HALF, (half + 1) * HALF)
                nc.scalar.copy(w_hi[:, slot, part_of], raw[:, slot, part_of]).then_inc(hi_done, 1)

            def hi_in(c, slot, half):
                hi(slot, half, None, 16 * c + 16, (unit_done, 6 * c - 4 + 2 * slot))

            def hi_mlp(f, par, down, half, used):
                hi(2 * par + down, half, None,
                   (8 * f + 16 * (6 if not (par and down) else 2) - 8 * par), used)

            def norm_stats(n, tb, ready):
                act.wait_ge(*ready)
                nc.scalar.activation(y_sb[:, tb, :], h_sb[:, tb, :], ACT.Square,
                                     accum_out=stat[:, TB * n + tb, 0:1]).then_inc(ss_done, 1)

            def norm_root(n, tb):
                act.wait_ge(var_done, TB * n + tb + 1)
                nc.scalar.activation(stat[:, TB * n + tb, 2:3], stat[:, TB * n + tb, 1:2], ACT.Sqrt
                                     ).then_inc(sd_done, 1)

            def yT_hi(n, tb):
                for b in range(2):
                    act.wait_ge(yt_done, 2 * (TB * n + tb) + b + 1)
                    nc.scalar.copy(yT[:, 4 * b:4 * b + 4, HI, tb * P:(tb + 1) * P],
                                   bank[NORM[tb][b]][:].rearrange("p (k n) -> p k n", k=4)).then_inc(yhi_done, 1)

            def v_copy(c, tb):
                act.wait_ge(unit_done, 6 * c + tb + 1)
                nc.scalar.copy(v_sb[:, tb, bass.ds(c * CW, CW)], bank[UNIT[tb]][:, 0:CW]).then_inc(v_ready, 1)

            def qk_part(c, u):
                act.wait_ge(unit_done, 6 * c + u + 1)
                nc.scalar.activation(part[:, u % 2, :], bank[UNIT[u % 2]][:, T:2 * T], ACT.Copy,
                                     scale=-SCALE if u < 4 else 1.0).then_inc(part_done, 1)

            def softmax_exp(a, s):
                act.wait_ge(biased, 4 * a + s + 1)
                p, h = s // 2, s % 2
                for tb, own in ((0, slice(0, P)), (1, slice(P, 3 * P))):
                    last = nc.scalar.activation(probs[:, s, own], probs[:, s, own], ACT.Exp,
                                                bias=negmax[:, p, 2 * tb + h:2 * tb + h + 1], scale=-1.0,
                                                accum_out=rowsum[:, p, 2 * tb + h:2 * tb + h + 1])
                last.then_inc(exp_done, 1)

            def out_hi(a, p):
                act.wait_ge(ot_done, 2 * a + p + 1)
                nc.scalar.copy(oT[:, bass.ds(a * 2 + p, 1), HI, :].rearrange("p a n -> p (a n)"),
                               bank[OTB][:, T - 1::-1]).then_inc(othi_done, 1)

            def up_part(f, i):
                act.wait_ge(up_done, 2 * f + i + 1)
                nc.scalar.copy(part[:, i, :], bank[UP[i]][:, T:2 * T]).then_inc(upart_done, 1)

            def h_hi(f, par, i):
                act.wait_ge(s_done, 2 * f + i + 1)
                nc.scalar.copy(hT[:, par, i, HI, :], s_sb[:, i, :]).then_inc(hhi_done, 1)

            def step(f, par, last=False):
                for half in range(2):
                    hi_mlp(f + 1, 1 - par, 1, half, (down_done, f) if not isinstance(f, int) or f else (wout_used, 4))
                for i in range(2):
                    up_part(f + 1, i)
                    if not last:
                        hi_mlp(f + 2, par, 0, i, (up_done, 2 * f + 2))
                    h_hi(f + 1, 1 - par, i)

            nc.scalar.preload_act_table(ACT.Sqrt)
            norm_stats(0, 0, (x_loaded[0], 16))
            norm_root(0, 0)
            norm_stats(0, 1, (x_loaded[1], 16))
            norm_root(0, 1)
            nc.scalar.preload_act_table(ACT.Exp)
            for half in range(2):
                hi(0, half, half, 16)
            yT_hi(0, 0)
            yT_hi(0, 1)
            for half in range(2):
                hi(1, half, 2 + half, 16)
            hi(2, 0, None, 16)
            v_copy(0, 0)
            hi(2, 1, None, 16)
            v_copy(0, 1)
            hi_in(1, 0, 0)
            qk_part(0, 2)
            hi_in(1, 0, 1)
            qk_part(0, 3)
            hi_in(1, 1, 0)
            qk_part(0, 4)
            hi_in(1, 1, 1)
            qk_part(0, 5)
            with act.Fori(1, CHUNKS_IN) as c:
                a = c - 1
                hi_in(c, 2, 0)
                softmax_exp(a, 0)
                softmax_exp(a, 1)
                hi_in(c, 2, 1)
                v_copy(c, 0)
                softmax_exp(a, 2)
                softmax_exp(a, 3)
                v_copy(c, 1)
                hi_in(c + 1, 0, 0)
                qk_part(c, 2)
                hi_in(c + 1, 0, 1)
                qk_part(c, 3)
                hi_in(c + 1, 1, 0)
                out_hi(a, 0)
                qk_part(c, 4)
                out_hi(a, 1)
                hi_in(c + 1, 1, 1)
                qk_part(c, 5)
            a = CHUNKS_IN - 1
            softmax_exp(a, 0)
            hi(2, 0, None, 16 * 5, (unit_done, 24))
            softmax_exp(a, 1)
            softmax_exp(a, 2)
            hi(2, 1, None, 16 * 5, (unit_done, 24))
            softmax_exp(a, 3)
            nc.scalar.preload_act_table(ACT.Sqrt)
            for half in range(2):
                hi(3, half, None, 16)
            out_hi(a, 0)
            out_hi(a, 1)
            for half in range(2):
                hi_mlp(0, 0, 0, half, (wout_used, 1))
            norm_stats(1, 0, (h_done, 1))
            norm_root(1, 0)
            for half in range(2):
                hi_mlp(0, 0, 1, half, (wout_used, 2))
            yT_hi(1, 0)
            norm_stats(1, 1, (h_done, 2))
            norm_root(1, 1)
            for half in range(2):
                hi_mlp(1, 1, 0, half, (wout_used, 3))
            yT_hi(1, 1)
            up_part(0, 0)
            h_hi(0, 0, 0)
            up_part(0, 1)
            h_hi(0, 0, 1)
            step(0, 0)
            step(1, 1)
            with act.Fori(2, CHUNKS_UP - 2, 2) as f:
                step(f, 0)
                step(f + 1, 1)
            step(CHUNKS_UP - 2, 0, last=True)
            for tb in range(TB):
                norm_stats(2, tb, (h2_done, tb + 1))
                norm_root(2, tb)

        @block.vector
        def _(dve):
            v = nc.vector

            def f32(ap):
                return ap.bitcast(F32)

            def lo(slot, half, count):
                dve.wait_ge(hi_done, count + 1)
                own = slice(half * HALF, (half + 1) * HALF)
                v.tensor_tensor(w_lo[:, slot, own], raw[:, slot, own], f32(w_hi[:, slot, own]), ALU.subtract
                                ).then_inc(lo_done, 1)

            def lo_in(c, slot, half):
                lo(slot, half, 6 * c + 2 * slot + half)

            def lo_mlp(f, par, down, half):
                lo(2 * par + down, half, 4 * f + 2 * MLP0 + 2 * down + half)

            def norm_var(n, tb):
                i = TB * n + tb
                dve.wait_ge(ss_done, i + 1)
                v.tensor_scalar(stat[:, i, 1:2], stat[:, i, 0:1], 1.0 / D, EPS, ALU.mult, ALU.add).then_inc(var_done, 1)

            def norm_rows(n, tb):
                i = TB * n + tb
                dve.wait_ge(sd_done, i + 1)
                v.reciprocal(stat[:, i, 3:4], stat[:, i, 2:3]).then_inc(rstd_done, 1)
                dve.wait_ge(rstd_done, i + 1)
                dve.wait_ge(gain_loaded, 16 * (n + 1))
                v.scalar_tensor_tensor(y_sb[:, tb, :], h_sb[:, tb, :], stat[:, i, 3:4], gain[:], ALU.mult, ALU.mult
                                       ).then_inc(out_ready if n == 2 else y_done, 1)

            def yT_lo(n, tb):
                for b in range(2):
                    dve.wait_ge(yhi_done, 2 * (TB * n + tb) + b + 1)
                    own = (slice(None), slice(4 * b, 4 * b + 4))
                    v.tensor_tensor(yT[:, 4 * b:4 * b + 4, LO, tb * P:(tb + 1) * P],
                                    bank[NORM[tb][b]][:].rearrange("p (k n) -> p k n", k=4),
                                    f32(yT[:, 4 * b:4 * b + 4, HI, tb * P:(tb + 1) * P]), ALU.subtract
                                    ).then_inc(ylo_done, 1)

            def qk_sum(c, u):
                dve.wait_ge(part_done, 4 * c + u - 1)
                dst = qT[:, u % 2, ::-1] if u < 4 else kT[:, u % 2, :]
                v.scalar_tensor_tensor(dst, bank[UNIT[u % 2]][:, 0:T], -SCALE if u < 4 else 1.0, part[:, u % 2, :],
                                       ALU.mult, ALU.add).then_inc(qk_ready, 1)

            def add_bias(a, s):
                if s == 0:
                    dve.wait_ge(bias_loaded, a * 16 + 16)
                dve.wait_ge(scores_done, 4 * a + s + 1)
                dve.sem_inc(scores_seen, 1)
                p, h = s // 2, s % 2
                for tb, own, bias in ((0, slice(0, P), slice(P, T)), (1, slice(P, 3 * P), slice(0, T))):
                    last = v.tensor_tensor_reduce(probs[:, s, own], bank[SCORE[s]][:, own], bias_sb[:, s, bias],
                                                  1.0, MASKED, ALU.add, ALU.min,
                                                  negmax[:, p, 2 * tb + h:2 * tb + h + 1])
                last.then_inc(biased, 1)

            def pT_copy(a, s):
                dve.wait_ge(pt_done, 4 * a + s + 1)
                v.tensor_copy(pT[:, s, :], bank[SCORE[s]][:, 0:3 * P]).then_inc(pt_ready, 1)

            def sum_inverse(a, p):
                dve.wait_ge(exp_done, 4 * a + 2 * p + 2)
                v.reciprocal(rinv[:, p, :], rowsum[:, p, :]).then_inc(rinv_done, 1)

            def out_rows_(a, p):
                dve.wait_ge(rinv_done, 2 * a + p + 1)
                dve.wait_ge(pv_done, 2 * a + p + 1)
                v.tensor_tensor(o_sb[:, p, :, :].rearrange("p t (h d) -> p (t h) d", h=2),
                                bank[PV][:, 0:T].rearrange("p (s d) -> p s d", s=4),
                                rinv[:, p, :].unsqueeze(2).to_broadcast([P, 4, DH]), ALU.mult).then_inc(o_ready, 1)

            def out_lo(a, p):
                dve.wait_ge(othi_done, 2 * a + p + 1)
                pair = bass.ds(a * 2 + p, 1)
                v.tensor_tensor(oT[:, pair, LO, :].rearrange("p a n -> p (a n)"), bank[OTB][:, T - 1::-1],
                                f32(oT[:, pair, HI, :].rearrange("p a n -> p (a n)")), ALU.subtract
                                ).then_inc(ot_ready, 1)

            def residual(tb, done, signal):
                dve.wait_ge(*done)
                for c in range(2):
                    own = slice(c * 512, (c + 1) * 512)
                    last = v.tensor_tensor(h_sb[:, tb, own], bank[ACC[tb][c]][:], h_sb[:, tb, own], ALU.add)
                last.then_inc(signal, 1)

            def up_sum(f, i):
                dve.wait_ge(upart_done, 2 * f + i + 1)
                v.tensor_tensor(z_sb[:, i, :], bank[UP[i]][:, 0:T], part[:, i, :], ALU.add).then_inc(z_done, 1)
                dve.wait_ge(z_done, 2 * f + i + 1)
                v.scalar_tensor_tensor(s_sb[:, i, :], z_sb[:, i, :], 0.0, z_sb[:, i, :], ALU.max, ALU.mult
                                       ).then_inc(s_done, 1)

            def h_lo(f, par, i):
                dve.wait_ge(hhi_done, 2 * f + i + 1)
                v.tensor_tensor(hT[:, par, i, LO, :], s_sb[:, i, :], f32(hT[:, par, i, HI, :]), ALU.subtract
                                ).then_inc(hT_ready, 1)

            def step(f, par, last=False):
                for half in range(2):
                    lo_mlp(f + 1, 1 - par, 1, half)
                for i in range(2):
                    up_sum(f + 1, i)
                    if not last:
                        lo_mlp(f + 2, par, 0, i)
                    h_lo(f + 1, 1 - par, i)

            for tb in range(TB):
                norm_var(0, tb)
                norm_rows(0, tb)
            for half in range(2):
                lo(0, half, half)
            dve.wait_ge(bias_summed, 1)
            v.scalar_tensor_tensor(bv_sb[:], bank[0][0:HEADS, 0:BV], -1.0, fill_sb[:], ALU.mult, ALU.add
                                   ).then_inc(bias_vec, 1)
            yT_lo(0, 0)
            yT_lo(0, 1)
            for half in range(2):
                lo(1, half, 2 + half)
            lo_in(0, 2, 0)
            lo_in(0, 2, 1)
            lo_in(1, 0, 0)
            qk_sum(0, 2)
            lo_in(1, 0, 1)
            qk_sum(0, 3)
            lo_in(1, 1, 0)
            qk_sum(0, 4)
            lo_in(1, 1, 1)
            qk_sum(0, 5)
            with dve.Fori(1, CHUNKS_IN) as c:
                a = c - 1
                add_bias(a, 0)
                add_bias(a, 1)
                lo_in(c, 2, 0)
                sum_inverse(a, 0)
                add_bias(a, 2)
                add_bias(a, 3)
                lo_in(c, 2, 1)
                pT_copy(a, 0)
                pT_copy(a, 1)
                lo_in(c + 1, 0, 0)
                sum_inverse(a, 1)
                qk_sum(c, 2)
                out_rows_(a, 0)
                pT_copy(a, 2)
                pT_copy(a, 3)
                lo_in(c + 1, 0, 1)
                qk_sum(c, 3)
                out_rows_(a, 1)
                lo_in(c + 1, 1, 0)
                out_lo(a, 0)
                qk_sum(c, 4)
                out_lo(a, 1)
                lo_in(c + 1, 1, 1)
                qk_sum(c, 5)
            a = CHUNKS_IN - 1
            for s in range(4):
                add_bias(a, s)
                if s % 2:
                    lo(2, s // 2, 2 * (OUT0 + 2) + s // 2)
                    sum_inverse(a, s // 2)
            for s in range(4):
                pT_copy(a, s)
            for half in range(2):
                lo(3, half, 2 * (OUT0 + 3) + half)
            out_rows_(a, 0)
            out_rows_(a, 1)
            out_lo(a, 0)
            out_lo(a, 1)
            for half in range(2):
                lo_mlp(0, 0, 0, half)
            residual(0, (mix_done, 1), h_done)
            norm_var(1, 0)
            norm_rows(1, 0)
            for half in range(2):
                lo_mlp(0, 0, 1, half)
            yT_lo(1, 0)
            residual(1, (wout_used, 4), h_done)
            norm_var(1, 1)
            norm_rows(1, 1)
            for half in range(2):
                lo_mlp(1, 1, 0, half)
            yT_lo(1, 1)
            for i in range(2):
                up_sum(0, i)
                h_lo(0, 0, i)
            step(0, 0)
            step(1, 1)
            with dve.Fori(2, CHUNKS_UP - 2, 2) as f:
                step(f, 0)
                step(f + 1, 1)
            step(CHUNKS_UP - 2, 0, last=True)
            for tb in range(TB):
                residual(tb, (mlp_done, tb + 1), h2_done)
                norm_var(2, tb)
                norm_rows(2, tb)


_INS = ["x", "rel_bias", "norm_mix", "norm_mlp", "mlp_up", "mlp_down", "a_w_in", "a_w_out", "final_norm"]


def kernel(**inputs):
    import concourse.bacc as _bacc
    from concourse.bass_utils import run_bass_kernel_spmd as _run

    nc = _bacc.Bacc("TRN2", target_bir_lowering=False, num_devices=1)
    arrays, args = {}, []
    for name, a in [(n, np.ascontiguousarray(inputs[n])) for n in _INS] + list(shape_constants().items()):
        arrays[f"in_{name}_dram"] = a
        args.append(nc.dram_tensor(f"in_{name}_dram", a.shape, mybir.dt.from_np(a.dtype), kind="ExternalInput").ap())
    out = nc.dram_tensor("out_0_dram", (1, T, D), F32, kind="ExternalOutput").ap()
    build(nc, *args, out)
    r = _run(nc, [arrays], core_ids=[0])
    return r.results[0]["out_0_dram"]
```

```python
from contextlib import ExitStack

import numpy as np

import concourse.bass as bass
from concourse import mybir

F32 = mybir.dt.float32
F32R = mybir.dt.float32r
ALU = mybir.AluOpType
ACT = mybir.ActivationFunctionType

P = 128
D = 1024
T = 256
TB = T // P
KB = D // P
HEADS = 16
DH = D // HEADS
PAIRS = HEADS // 2
F = 4 * D
CW = 256
CHUNKS_IN = D // CW
CHUNKS_OUT = D // CW
CHUNKS_UP = F // CW
CE = D * CW // P
HALF = CE // 2
SLOTS = 4
OUT0 = 3 * CHUNKS_IN
MLP0 = OUT0 + CHUNKS_OUT
UNITS = 6
BUCKETS = 32
MAX_DIST = 128
BV = P + T
EPS = 1e-6
MASKED = 3.0e38
SCALE = DH ** -0.5
HI, LO = 0, 1


def shape_constants():
    dist = T - 1 - np.arange(BV)
    n = np.maximum(dist, 0)
    exact = BUCKETS // 2
    large = exact + (np.log(np.maximum(n, 1) / exact) / np.log(MAX_DIST / exact) * (BUCKETS - exact)).astype(np.int64)
    bucket = np.where(n < exact, n, np.minimum(large, BUCKETS - 1))
    onehot = (np.arange(BUCKETS)[:, None] == bucket[None, :]) & (dist >= 0)[None, :]
    fill = np.broadcast_to(np.where(dist < 0, MASKED, 0.0), (HEADS, BV))
    return {
        "identity": np.eye(P, dtype=np.float32),
        "bucket_onehot": onehot.astype(np.float32),
        "causal_fill": np.ascontiguousarray(fill, dtype=np.float32),
    }


def build(nc, x, rel_bias, norm_mix, norm_mlp, mlp_up, mlp_down, w_in, w_out, final_norm,
          identity, bucket_onehot, causal_fill, out):
    x_rows = x[0].rearrange("(b p) d -> b p d", p=P)
    out_rows = out[0].rearrange("(b p) d -> b p d", p=P)
    w_in_v = w_in[0].rearrange("(k p) n -> p k n", p=P)
    w_out_v = w_out[0].rearrange("(k p) n -> p k n", p=P)
    up_v = mlp_up[0].rearrange("(k p) n -> p k n", p=P)
    down_v = mlp_down[0].rearrange("(k p) n -> p k n", p=P)
    bias_dram = nc.dram_tensor("bias_by_distance", [HEADS, BV], F32, kind="Internal").ap()

    with ExitStack() as ctx:
        def sb(name, shape, dt=F32):
            return ctx.enter_context(nc.sbuf_tensor(name, shape, dt))

        def sem(name):
            return ctx.enter_context(nc.semaphore(name))

        h_sb = sb("h_sb", [P, TB, D])
        y_sb = sb("y_sb", [P, TB, D])
        yT = sb("yT", [P, KB, 2, T], F32R)
        raw = sb("raw", [P, SLOTS, CE])
        w_hi = sb("w_hi", [P, SLOTS, CE], F32R)
        w_lo = sb("w_lo", [P, SLOTS, CE], F32R)
        qT = sb("qT", [P, 2, T])
        kT = sb("kT", [P, 2, T])
        v_sb = sb("v_sb", [P, TB, D])
        bias_sb = sb("bias_sb", [P, 4, T])
        probs = sb("probs", [P, 4, 3 * P])
        pT = sb("pT", [P, 4, 3 * P])
        o_sb = sb("o_sb", [P, 2, TB, P])
        oT = sb("oT", [P, PAIRS, 2, T], F32R)
        negmax = sb("negmax", [P, 2, 4])
        rowsum = sb("rowsum", [P, 2, 4])
        rinv = sb("rinv", [P, 2, 4])
        part = sb("part", [P, 2, T])
        z_sb = sb("z_sb", [P, 2, T])
        s_sb = sb("s_sb", [P, 2, T])
        hT = sb("hT", [P, 2, 2, 2, T], F32R)
        gain = sb("gain", [P, D])
        squares = sb("squares", [P, 2, 512])
        ones = sb("ones", [1, P])
        ident = sb("ident", [P, P])
        rel_sb = sb("rel_sb", [BUCKETS, HEADS])
        onehot_sb = sb("onehot_sb", [BUCKETS, BV])
        fill_sb = sb("fill_sb", [HEADS, BV])
        bv_sb = sb("bv_sb", [HEADS, BV])
        stat = sb("stat", [P, 6, 5])
        SS0, SS1, PART_VAR, SD, RSTD = range(5)

        bank = [ctx.enter_context(nc.psum_tensor(f"bank{i}", [P, 512], F32)) for i in range(8)]
        UNIT = [0, 1]
        SCORE = [2, 3, 4, 5]
        PV, OTB = 6, 7
        GAIN = [2, 3]
        BIAS = 2
        ACC = [[0, 1], [2, 3]]
        UP = [4, 5]
        NORM = [[4, 5], [6, 7]]

        raw_full = [sem(f"raw_full{i}") for i in range(SLOTS)]
        x_loaded = [sem(f"x_loaded{i}") for i in range(TB)]
        ident_loaded, tables_loaded = sem("ident_loaded"), sem("tables_loaded")
        gain_first, gain_next, bias_loaded = sem("gain_first"), sem("gain_next"), sem("bias_loaded")
        bias_summed, bias_vec, bias_stored = sem("bias_summed"), sem("bias_vec"), sem("bias_stored")
        raw_first, gain_spread, ones_made = sem("raw_first"), sem("gain_spread"), sem("ones_made")
        raw_free, scores_seen = sem("raw_free"), sem("scores_seen")
        hi_done, lo_done = sem("hi_done"), sem("lo_done")
        ss_early, ss_late, var_done, sd_done = sem("ss_early"), sem("ss_late"), sem("var_done"), sem("sd_done")
        gained = sem("gained")
        rstd_done, y_done = sem("rstd_done"), sem("y_done")
        yt_done, yhi_done, ylo_done = sem("yt_done"), sem("yhi_done"), sem("ylo_done")
        unit_done, v_ready, part_done, qk_ready = sem("unit_done"), sem("v_ready"), sem("part_done"), sem("qk_ready")
        scores_done, biased, exp_done = sem("scores_done"), sem("biased"), sem("exp_done")
        pt_done, pt_ready = sem("pt_done"), sem("pt_ready")
        rinv_done, pv_done, o_ready = sem("rinv_done"), sem("pv_done"), sem("o_ready")
        ot_done, othi_done, ot_ready = sem("ot_done"), sem("othi_done"), sem("ot_ready")
        mix_done, wout_used, h_done = sem("mix_done"), sem("wout_used"), sem("h_done")
        up_done, upart_done, z_done = sem("up_done"), sem("upart_done"), sem("z_done")
        s_done, hhi_done, hT_ready = sem("s_done"), sem("hhi_done"), sem("hT_ready")
        down_done, mlp_done, h2_done = sem("down_done"), sem("mlp_done"), sem("h2_done")
        out_ready, stored = sem("out_ready"), sem("stored")

        block = ctx.enter_context(nc.Block())

        def cols(slot_tensor, slot):
            return slot_tensor[:, slot, :].rearrange("p (k n) -> p k n", k=KB)

        def rows(slot_tensor, slot):
            return slot_tensor[:, slot, :].rearrange("p (k n) -> p k n", k=2)

        @block.sync
        def _(sp):
            def load(slot, src, split):
                if split is not None:
                    sp.wait_ge(lo_done, split)
                    sp.sem_inc(raw_free, 1)
                n = CE // src.shape[1]
                nc.sync.dma_start(raw[:, slot, :].rearrange("p (k n) -> p k n", n=n), src
                                  ).then_inc(raw_full[slot], 16)

            nc.sync.dma_start(gain[0:1, :], norm_mix).then_inc(gain_first, 16)
            nc.sync.dma_start(h_sb[:, 0, :], x_rows[0]).then_inc(x_loaded[0], 16)
            nc.sync.dma_start(ident[:], identity).then_inc(ident_loaded, 16)
            nc.sync.dma_start(cols(raw, 0)[:, 0:4, :], w_in_v[:, 0:4, 2 * D:2 * D + CW]).then_inc(raw_first, 16)
            nc.sync.dma_start(h_sb[:, 1, :], x_rows[1]).then_inc(x_loaded[1], 16)
            nc.sync.dma_start(cols(raw, 0)[:, 4:8, :], w_in_v[:, 4:8, 2 * D:2 * D + CW]).then_inc(raw_full[0], 16)
            load(1, w_in_v[:, :, 0:CW], None)
            load(2, w_in_v[:, :, D:D + CW], None)
            load(3, w_out_v[:, 6:8, :], None)
            with sp.Fori(1, CHUNKS_IN) as c:
                for slot, base in enumerate((2 * D, 0, D)):
                    load(slot, w_in_v[:, :, bass.ds(c * CW + base, CW)], 6 * c - 4 + 2 * slot)
            for q in range(3):
                load(q, w_out_v[:, 2 * q:2 * q + 2, :], 2 * (OUT0 + q - 3 + 1))
            with sp.Fori(0, CHUNKS_UP // 2) as i:
                for r in range(2):
                    load(2 * r, up_v[:, :, bass.ds(i * 2 * CW + r * CW, CW)], 8 * i + 26 + 4 * r)
                    load(2 * r + 1, down_v[:, bass.ds(i * 4 + 2 * r, 2), :], 8 * i + 28 + 4 * r)
            for tb in range(TB):
                for b in range(2):
                    own = slice(b * 512, (b + 1) * 512)
                    sp.wait_ge(out_ready, 2 * tb + b + 1)
                    nc.sync.dma_start(out_rows[tb][:, own], y_sb[:, tb, own]).then_inc(stored, 16)
            sp.wait_ge(stored, 16 * 2 * TB)
            sp.wait_ge(bias_stored, 16)

        @block.gpsimd
        def _(pool):
            nc.gpsimd.dma_start(rel_sb[:], rel_bias).then_inc(tables_loaded, 16)
            nc.gpsimd.dma_start(onehot_sb[:], bucket_onehot).then_inc(tables_loaded, 16)
            nc.gpsimd.dma_start(fill_sb[:], causal_fill).then_inc(tables_loaded, 16)
            pool.wait_ge(bias_vec, 1)
            nc.gpsimd.dma_start(bias_dram, bv_sb[:]).then_inc(bias_stored, 16)
            pool.wait_ge(bias_stored, 16)

            def tiles(a):
                src = bass.AP(tensor=bias_dram.tensor, offset=bias_dram.offset + a * (4 * BV),
                              ap=[[1, P], [BV, 4], [1, T]])
                nc.gpsimd.dma_start(bias_sb[:], src).then_inc(bias_loaded, 16)

            tiles(0)
            pool.wait_ge(y_done, 2 * TB)
            nc.gpsimd.dma_start(gain[:], norm_mlp.partition_broadcast(P).rearrange("p a d -> p (a d)")
                                ).then_inc(gain_next, 16)
            with pool.Fori(1, CHUNKS_IN) as a:
                pool.wait_ge(biased, 4 * a)
                tiles(a)
            pool.wait_ge(gained, 2 * TB)
            nc.gpsimd.dma_start(gain[:], final_norm.partition_broadcast(P)).then_inc(gain_next, 16)

        @block.tensor
        def _(pe):
            mm = nc.tensor.matmul

            def transposes(norm, tb):
                if norm == 0 and tb == 0:
                    pe.wait_ge(ident_loaded, 16)
                for b in range(2):
                    pe.wait_ge(y_done, 2 * (norm * TB + tb) + b + 1)
                    for k in range(4):
                        last = nc.tensor.transpose(bank[NORM[tb][b]][:, k * P:(k + 1) * P],
                                                   y_sb[:, tb, (4 * b + k) * P:(4 * b + k + 1) * P], ident[:])
                    last.then_inc(yt_done, 1)

            def v_unit(c, tb, first):
                if not first:
                    pe.wait_ge(lo_done, 6 * c + 2)
                    pe.wait_ge(qk_ready, 4 * c - 1 + tb)
                wh, wl = cols(w_hi, 0), cols(w_lo, 0)
                acc = bank[UNIT[tb]][:, 0:CW]
                tok = slice(tb * P, (tb + 1) * P)
                for k in range(KB):
                    if first and k % 4 == 0:
                        pe.wait_ge(ylo_done, 2 * tb + k // 4 + 1)
                        if k and tb == 0:
                            transposes(0, 1)
                        pe.wait_ge(lo_done, k // 4 + 1)
                    mm(acc, yT[:, k, HI, tok], wh[:, k, :], start=(k == 0), stop=False)
                    mm(acc, yT[:, k, HI, tok], wl[:, k, :], start=False, stop=False)
                    last = mm(acc, yT[:, k, LO, tok], wh[:, k, :], start=False, stop=(k == KB - 1))
                last.then_inc(unit_done, 1)

            def qk_unit(c, u):
                slot = u // 2
                pe.wait_ge(lo_done, 6 * c + 2 * slot + 2)
                if u < 4:
                    pe.wait_ge(v_ready, 2 * c + u - 1)
                else:
                    pe.wait_ge(qk_ready, 4 * c + u - 3)
                feature_unit(bank[UNIT[u % 2]], slot, u % 2).then_inc(unit_done, 1)

            def feature_unit(dst, slot, i):
                wh, wl = cols(w_hi, slot), cols(w_lo, slot)
                own = slice(i * P, (i + 1) * P)
                for k in range(KB):
                    mm(dst[:], wh[:, k, own], yT[:, k, :, :], start=(k == 0), stop=False, skip_group_check=True)
                    last = mm(dst[:, 0:T], wl[:, k, own], yT[:, k, HI, :], start=False, stop=(k == KB - 1),
                              skip_group_check=True)
                return last

            def scores(a, p):
                pe.wait_ge(qk_ready, 4 * a + 3 + p)
                heads = [(bank[SCORE[2 * p + h]], slice(h * DH, (h + 1) * DH)) for h in range(2)]
                for dst, dims in heads:
                    mm(dst[:, 0:P], qT[dims, p, P:T], kT[dims, p, 0:P], start=True, stop=True)
                for dst, dims in heads:
                    mm(dst[:, P:3 * P], qT[dims, p, 0:P], kT[dims, p, :], start=True, stop=True
                       ).then_inc(scores_done, 1)

            def probs_T(a, p):
                for h in range(2):
                    pe.wait_ge(exp_done, 4 * a + 2 * p + h + 1)
                    for b in range(3):
                        last = nc.tensor.transpose(bank[SCORE[2 * p + h]][:, b * P:(b + 1) * P],
                                                   probs[:, 2 * p + h, b * P:(b + 1) * P], ident[:])
                    last.then_inc(pt_done, 1)

            def values(a, p):
                if p == 1:
                    pe.wait_ge(o_ready, 2 * a + 1)
                for h in range(2):
                    s = 2 * p + h
                    pe.wait_ge(pt_ready, 4 * a + s + 1)
                    vcol = bass.ds(a * (4 * DH) + s * DH, DH)
                    o0 = bank[PV][:, h * DH:(h + 1) * DH]
                    o1 = bank[PV][:, P + h * DH:P + (h + 1) * DH]
                    mm(o0, pT[:, s, 0:P], v_sb[:, 0, vcol], start=True, stop=True)
                    mm(o1, pT[:, s, P:2 * P], v_sb[:, 0, vcol], start=True, stop=False)
                    last = mm(o1, pT[:, s, 2 * P:3 * P], v_sb[:, 1, vcol], start=False, stop=True)
                last.then_inc(pv_done, 1)

            def out_T(a, p):
                pe.wait_ge(o_ready, 2 * a + p + 1)
                if p == 1:
                    pe.wait_ge(ot_ready, 2 * a + 1)
                for tb in range(TB):
                    last = nc.tensor.transpose(bank[OTB][:, (1 - tb) * P:(2 - tb) * P], o_sb[:, p, tb, :], ident[:])
                last.then_inc(ot_done, 1)

            def accumulate(lhs, slot, r, tb, start, stop, halves=(0, 1)):
                wh, wl = rows(w_hi, slot), rows(w_lo, slot)
                for l, w, first in ((HI, wh, start), (HI, wl, False), (LO, wh, False)):
                    for c in halves:
                        last = mm(bank[ACC[tb][c]][:], lhs(l), w[:, r, c * 512:(c + 1) * 512],
                                  start=first, stop=(stop and l == LO))
                return last

            def mix(tb, k):
                q = k // 2
                pe.wait_ge(lo_done, 2 * (OUT0 + q) + 2)
                pe.wait_ge(ot_ready, k + 1)
                last = accumulate(lambda l: oT[:, k, l, tb * P:(tb + 1) * P], q, k % 2, tb, k == 0, False)
                if tb == 1 and k % 2:
                    last.then_inc(wout_used, 1)

            def mix_last(tb):
                pe.wait_ge(lo_done, 2 * MLP0)
                pe.wait_ge(ot_ready, PAIRS)
                for c in range(2):
                    for k in (PAIRS - 2, PAIRS - 1):
                        last = accumulate(lambda l: oT[:, k, l, tb * P:(tb + 1) * P], 3, k % 2, tb, False,
                                          k == PAIRS - 1, (c,))
                    last.then_inc(mix_done, 1)

            def up(f, par, i):
                pe.wait_ge(lo_done, 4 * f + 2 * MLP0 + 2)
                feature_unit(bank[UP[i]], 2 * par, i).then_inc(up_done, 1)

            def up_first(i, tb):
                pe.wait_ge(lo_done, 2 * MLP0 + 2)
                wh, wl = cols(w_hi, 0), cols(w_lo, 0)
                own = slice(i * P, (i + 1) * P)
                dst = bank[UP[i]][:, tb * T:(tb + 1) * T].rearrange("p (l n) -> p l n", l=2)
                for k in range(KB):
                    if k % 4 == 0:
                        pe.wait_ge(ylo_done, 2 * (TB + tb) + k // 4 + 1)
                    y = yT[:, k, :, tb * P:(tb + 1) * P]
                    mm(dst, wh[:, k, own], y, start=(k == 0), stop=False)
                    last = mm(dst, wl[:, k, own], y, start=False, stop=(k == KB - 1))
                if tb == TB - 1:
                    last.then_inc(up_done, 1)

            def down(f, par, tb, start=False):
                if tb == 0:
                    pe.wait_ge(lo_done, 4 * f + 2 * MLP0 + 4)
                    pe.wait_ge(hT_ready, 2 * f + 2)
                for i in range(2):
                    last = accumulate(lambda l: hT[:, par, i, l, tb * P:(tb + 1) * P], 2 * par + 1, i, tb,
                                      start and i == 0, False)
                return last

            def down_last(tb):
                pe.wait_ge(lo_done, 4 * CHUNKS_UP + 2 * MLP0)
                pe.wait_ge(hT_ready, 2 * CHUNKS_UP)
                for c in range(2):
                    for i in range(2):
                        last = accumulate(lambda l: hT[:, 1, i, l, tb * P:(tb + 1) * P], 3, i, tb, False,
                                          i == 1, (c,))
                    last.then_inc(mlp_done, 1)

            def step(f, par, start=False):
                for i in range(2):
                    pe.wait_ge(z_done, 2 * f + i + 1)
                    up(f + 1, 1 - par, i)
                down(f, par, 0, start)
                down(f, par, 1, start).then_inc(down_done, 1)

            pe.wait_ge(ones_made, 1)
            pe.wait_ge(gain_first, 16)
            for b in range(2):
                last = mm(bank[GAIN[b]][:], ones[:], gain[0:1, b * 512:(b + 1) * 512], start=True, stop=True)
            last.then_inc(gain_spread, 1)
            transposes(0, 0)
            v_unit(0, 0, True)
            v_unit(0, 1, True)
            pe.wait_ge(tables_loaded, 48)
            mm(bank[BIAS][0:HEADS, 0:BV], rel_sb[:], onehot_sb[:], start=True, stop=True).then_inc(bias_summed, 1)
            for u in range(2, UNITS):
                qk_unit(0, u)
            with pe.Fori(1, CHUNKS_IN) as c:
                scores(c - 1, 0)
                v_unit(c, 0, False)
                scores(c - 1, 1)
                v_unit(c, 1, False)
                probs_T(c - 1, 0)
                qk_unit(c, 2)
                values(c - 1, 0)
                probs_T(c - 1, 1)
                qk_unit(c, 3)
                values(c - 1, 1)
                out_T(c - 1, 0)
                qk_unit(c, 4)
                out_T(c - 1, 1)
                qk_unit(c, 5)
            a = CHUNKS_IN - 1
            scores(a, 0)
            scores(a, 1)
            for k in range(4):
                mix(0, k)
            probs_T(a, 0)
            probs_T(a, 1)
            mix(0, 4)
            values(a, 0)
            mix(0, 5)
            values(a, 1)
            out_T(a, 0)
            mix(1, 0)
            out_T(a, 1)
            mix(1, 1)
            mix_last(0)
            for k in range(2, PAIRS - 2):
                mix(1, k)
            transposes(1, 0)
            mix_last(1)
            for i in range(2):
                up_first(i, 0)
            transposes(1, 1)
            for i in range(2):
                up_first(i, 1)
            step(0, 0, True)
            step(1, 1)
            with pe.Fori(2, CHUNKS_UP - 2, 2) as f:
                step(f, 0)
                step(f + 1, 1)
            f = CHUNKS_UP - 2
            for i in range(2):
                pe.wait_ge(z_done, 2 * f + i + 1)
                up(f + 1, 1, i)
            down(f, 0, 0)
            down_last(0)
            down(f, 0, 1)
            down_last(1)

        @block.scalar
        def _(act):
            def hi(slot, half, full, used=None):
                act.wait_ge(raw_full[slot], full)
                if used is not None:
                    act.wait_ge(used[0], used[1])
                part_of = slice(half * HALF, (half + 1) * HALF)
                nc.scalar.copy(w_hi[:, slot, part_of], raw[:, slot, part_of]).then_inc(hi_done, 1)

            def hi_in(c, slot, half):
                hi(slot, half, 16 * c + 16, (unit_done, 6 * c - 4 + 2 * slot))

            def hi_mlp(f, par, down, half, used):
                hi(2 * par + down, half, 8 * (f - par) + 16 * (2 if par and down else 6), used)

            def norm_square(n, tb, b, ready, signal):
                act.wait_ge(*ready)
                own = slice(b * 512, (b + 1) * 512)
                nc.scalar.activation(squares[:, b, :], h_sb[:, tb, own], ACT.Square,
                                     accum_out=stat[:, TB * n + tb, SS0 + b:SS0 + b + 1]).then_inc(signal, 1)

            def norm_root(n, tb, late):
                i = TB * n + tb
                act.wait_ge(ss_late, i + 1)
                act.wait_ge(var_done, i + 1)
                nc.scalar.activation(stat[:, i, SD:SD + 1], stat[:, i, SS0 + late:SS0 + late + 1], ACT.Sqrt,
                                     scale=1.0 / D, bias=stat[:, i, PART_VAR:PART_VAR + 1]).then_inc(sd_done, 1)

            def yT_hi(n, tb):
                for b in range(2):
                    act.wait_ge(yt_done, 2 * (TB * n + tb) + b + 1)
                    nc.scalar.copy(yT[:, 4 * b:4 * b + 4, HI, tb * P:(tb + 1) * P],
                                   bank[NORM[tb][b]][:].rearrange("p (k n) -> p k n", k=4)).then_inc(yhi_done, 1)

            def v_copy(c, tb):
                act.wait_ge(unit_done, 6 * c + tb + 1)
                nc.scalar.copy(v_sb[:, tb, bass.ds(c * CW, CW)], bank[UNIT[tb]][:, 0:CW]).then_inc(v_ready, 1)

            def qk_part(c, u):
                act.wait_ge(unit_done, 6 * c + u + 1)
                nc.scalar.activation(part[:, u % 2, :], bank[UNIT[u % 2]][:, T:2 * T], ACT.Copy,
                                     scale=-SCALE if u < 4 else 1.0).then_inc(part_done, 1)

            def softmax_exp(a, s):
                act.wait_ge(biased, 4 * a + s + 1)
                p, h = s // 2, s % 2
                for tb, own in ((0, slice(0, P)), (1, slice(P, 3 * P))):
                    last = nc.scalar.activation(probs[:, s, own], probs[:, s, own], ACT.Exp,
                                                bias=negmax[:, p, 2 * tb + h:2 * tb + h + 1], scale=-1.0,
                                                accum_out=rowsum[:, p, 2 * tb + h:2 * tb + h + 1])
                last.then_inc(exp_done, 1)

            def out_hi(a, p):
                act.wait_ge(ot_done, 2 * a + p + 1)
                nc.scalar.copy(oT[:, bass.ds(a * 2 + p, 1), HI, :].rearrange("p a n -> p (a n)"),
                               bank[OTB][:, T - 1::-1]).then_inc(othi_done, 1)

            def up_part(f, i, lo_half=None):
                act.wait_ge(up_done, 2 * f + i + 1)
                if lo_half is None:
                    nc.scalar.copy(part[:, i, :], bank[UP[i]][:, T:2 * T]).then_inc(upart_done, 1)
                else:
                    nc.scalar.copy(part[:, i, :].rearrange("p (b n) -> p b n", b=TB), lo_half).then_inc(upart_done, 1)

            def h_hi(f, par, i):
                act.wait_ge(s_done, 2 * f + i + 1)
                nc.scalar.copy(hT[:, par, i, HI, :], s_sb[:, i, :]).then_inc(hhi_done, 1)

            def step(f, par, first=False, last=False):
                for half in range(2):
                    hi_mlp(f + 1, 1 - par, 1, half, (mix_done, 4) if first else (down_done, f))
                for i in range(2):
                    up_part(f + 1, i)
                    if not last:
                        hi_mlp(f + 2, par, 0, i, (up_done, 2 * f + 2))
                    h_hi(f + 1, 1 - par, i)

            nc.scalar.preload_act_table(ACT.Sqrt)
            for tb in range(TB):
                norm_square(0, tb, 0, (x_loaded[tb], 16), ss_late)
                norm_root(0, tb, 0)
                if tb == 0:
                    act.wait_ge(raw_first, 16)
                    nc.scalar.copy(w_hi[:, 0, 0:HALF], raw[:, 0, 0:HALF]).then_inc(hi_done, 1)
                else:
                    hi(0, 1, 16)
                yT_hi(0, tb)
            nc.scalar.preload_act_table(ACT.Exp)
            for half in range(2):
                hi(1, half, 16)
            hi(2, 0, 16)
            v_copy(0, 0)
            hi(2, 1, 16)
            v_copy(0, 1)
            hi_in(1, 0, 0)
            qk_part(0, 2)
            hi_in(1, 0, 1)
            qk_part(0, 3)
            hi_in(1, 1, 0)
            qk_part(0, 4)
            hi_in(1, 1, 1)
            qk_part(0, 5)
            with act.Fori(1, CHUNKS_IN) as c:
                a = c - 1
                hi_in(c, 2, 0)
                softmax_exp(a, 0)
                softmax_exp(a, 1)
                hi_in(c, 2, 1)
                v_copy(c, 0)
                softmax_exp(a, 2)
                softmax_exp(a, 3)
                v_copy(c, 1)
                hi_in(c + 1, 0, 0)
                qk_part(c, 2)
                hi_in(c + 1, 0, 1)
                qk_part(c, 3)
                hi_in(c + 1, 1, 0)
                out_hi(a, 0)
                qk_part(c, 4)
                out_hi(a, 1)
                hi_in(c + 1, 1, 1)
                qk_part(c, 5)
            a = CHUNKS_IN - 1
            softmax_exp(a, 0)
            hi(2, 0, 16 * 5, (unit_done, 24))
            softmax_exp(a, 1)
            softmax_exp(a, 2)
            hi(2, 1, 16 * 5, (unit_done, 24))
            softmax_exp(a, 3)
            nc.scalar.preload_act_table(ACT.Sqrt)
            for half in range(2):
                hi(3, half, 16)
            out_hi(a, 0)
            out_hi(a, 1)
            for half in range(2):
                hi_mlp(0, 0, 0, half, (wout_used, 1))
            norm_square(1, 0, 0, (h_done, 1), ss_early)
            norm_square(1, 0, 1, (h_done, 2), ss_late)
            norm_root(1, 0, 1)
            for half in range(2):
                hi_mlp(0, 0, 1, half, (wout_used, 2))
            yT_hi(1, 0)
            hi_mlp(1, 1, 0, 0, (wout_used, 3))
            norm_square(1, 1, 0, (h_done, 3), ss_early)
            norm_square(1, 1, 1, (h_done, 4), ss_late)
            norm_root(1, 1, 1)
            hi_mlp(1, 1, 0, 1, (wout_used, 3))
            yT_hi(1, 1)
            for i in range(2):
                up_part(0, i, bank[UP[i]][:].rearrange("p (b l n) -> p b l n", b=TB, l=2)[:, :, LO, :])
                h_hi(0, 0, i)
            step(0, 0, first=True)
            step(1, 1)
            with act.Fori(2, CHUNKS_UP - 2, 2) as f:
                step(f, 0)
                step(f + 1, 1)
            step(CHUNKS_UP - 2, 0, last=True)
            for tb in range(TB):
                norm_square(2, tb, 0, (h2_done, 2 * tb + 1), ss_early)
                norm_square(2, tb, 1, (h2_done, 2 * tb + 2), ss_late)
                norm_root(2, tb, 1)

        @block.vector
        def _(dve):
            v = nc.vector

            def f32(ap):
                return ap.bitcast(F32)

            def lo(slot, half, count):
                dve.wait_ge(hi_done, count + 1)
                own = slice(half * HALF, (half + 1) * HALF)
                v.tensor_tensor(w_lo[:, slot, own], raw[:, slot, own], f32(w_hi[:, slot, own]), ALU.subtract
                                ).then_inc(lo_done, 1)

            def lo_in(c, slot, half):
                lo(slot, half, 6 * c + 2 * slot + half)

            def lo_mlp(f, par, down, half):
                lo(2 * par + down, half, 4 * f + 2 * MLP0 + 2 * down + half)

            def norm_var(n, tb, early, ready):
                i = TB * n + tb
                dve.wait_ge(*ready)
                v.tensor_scalar(stat[:, i, PART_VAR:PART_VAR + 1], stat[:, i, SS0 + early:SS0 + early + 1],
                                1.0 / D, EPS, ALU.mult, ALU.add).then_inc(var_done, 1)

            def gain_rows(n, tb):
                if tb == 0:
                    dve.wait_ge(gain_next, 16 * n)
                for b in range(2):
                    dve.wait_ge(h_done if n == 1 else h2_done, 2 * tb + b + 1)
                    own = slice(b * 512, (b + 1) * 512)
                    v.tensor_tensor(y_sb[:, tb, own], h_sb[:, tb, own], gain[:, own], ALU.mult
                                    ).then_inc(gained, 1)

            def scale_rows(n, tb, b):
                i = TB * n + tb
                if b == 0:
                    dve.wait_ge(sd_done, i + 1)
                    v.reciprocal(stat[:, i, RSTD:RSTD + 1], stat[:, i, SD:SD + 1]).then_inc(rstd_done, 1)
                    dve.wait_ge(gained, 2 * (i - TB) + 2)
                    dve.wait_ge(rstd_done, i + 1)
                own = slice(b * 512, (b + 1) * 512)
                v.tensor_scalar(y_sb[:, tb, own], y_sb[:, tb, own], stat[:, i, RSTD:RSTD + 1], None, ALU.mult
                                ).then_inc(out_ready if n == 2 else y_done, 1)

            def norm_rows(i):
                dve.wait_ge(sd_done, i + 1)
                v.reciprocal(stat[:, i, RSTD:RSTD + 1], stat[:, i, SD:SD + 1]).then_inc(rstd_done, 1)
                dve.wait_ge(gain_spread, 1)
                dve.wait_ge(rstd_done, i + 1)
                for b in range(2):
                    own = slice(b * 512, (b + 1) * 512)
                    v.scalar_tensor_tensor(y_sb[:, i, own], h_sb[:, i, own], stat[:, i, RSTD:RSTD + 1],
                                           bank[GAIN[b]][:], ALU.mult, ALU.mult).then_inc(y_done, 1)

            def yT_lo(n, tb):
                for b in range(2):
                    dve.wait_ge(yhi_done, 2 * (TB * n + tb) + b + 1)
                    v.tensor_tensor(yT[:, 4 * b:4 * b + 4, LO, tb * P:(tb + 1) * P],
                                    bank[NORM[tb][b]][:].rearrange("p (k n) -> p k n", k=4),
                                    f32(yT[:, 4 * b:4 * b + 4, HI, tb * P:(tb + 1) * P]), ALU.subtract
                                    ).then_inc(ylo_done, 1)

            def qk_sum(c, u):
                dve.wait_ge(part_done, 4 * c + u - 1)
                dst = qT[:, u % 2, ::-1] if u < 4 else kT[:, u % 2, :]
                v.scalar_tensor_tensor(dst, bank[UNIT[u % 2]][:, 0:T], -SCALE if u < 4 else 1.0, part[:, u % 2, :],
                                       ALU.mult, ALU.add).then_inc(qk_ready, 1)

            def add_bias(a, s):
                if s == 0:
                    dve.wait_ge(bias_loaded, a * 16 + 16)
                dve.wait_ge(scores_done, 4 * a + s + 1)
                dve.sem_inc(scores_seen, 1)
                p, h = s // 2, s % 2
                for tb, own, bias in ((0, slice(0, P), slice(P, T)), (1, slice(P, 3 * P), slice(0, T))):
                    last = v.tensor_tensor_reduce(probs[:, s, own], bank[SCORE[s]][:, own], bias_sb[:, s, bias],
                                                  1.0, MASKED, ALU.add, ALU.min,
                                                  negmax[:, p, 2 * tb + h:2 * tb + h + 1])
                last.then_inc(biased, 1)

            def pT_copy(a, s):
                dve.wait_ge(pt_done, 4 * a + s + 1)
                v.tensor_copy(pT[:, s, :], bank[SCORE[s]][:, 0:3 * P]).then_inc(pt_ready, 1)

            def sum_inverse(a, p):
                dve.wait_ge(exp_done, 4 * a + 2 * p + 2)
                v.reciprocal(rinv[:, p, :], rowsum[:, p, :]).then_inc(rinv_done, 1)

            def out_rows_(a, p):
                dve.wait_ge(rinv_done, 2 * a + p + 1)
                dve.wait_ge(pv_done, 2 * a + p + 1)
                v.tensor_tensor(o_sb[:, p, :, :].rearrange("p t (h d) -> p (t h) d", h=2),
                                bank[PV][:, 0:T].rearrange("p (s d) -> p s d", s=4),
                                rinv[:, p, :].unsqueeze(2).to_broadcast([P, 4, DH]), ALU.mult).then_inc(o_ready, 1)

            def out_lo(a, p):
                dve.wait_ge(othi_done, 2 * a + p + 1)
                pair = bass.ds(a * 2 + p, 1)
                v.tensor_tensor(oT[:, pair, LO, :].rearrange("p a n -> p (a n)"), bank[OTB][:, T - 1::-1],
                                f32(oT[:, pair, HI, :].rearrange("p a n -> p (a n)")), ALU.subtract
                                ).then_inc(ot_ready, 1)

            def residual(tb, c, done, signal):
                dve.wait_ge(done, 2 * tb + c + 1)
                own = slice(c * 512, (c + 1) * 512)
                v.tensor_tensor(h_sb[:, tb, own], bank[ACC[tb][c]][:], h_sb[:, tb, own], ALU.add).then_inc(signal, 1)

            def up_sum(f, i, hi_half=None):
                dve.wait_ge(upart_done, 2 * f + i + 1)
                if hi_half is None:
                    v.tensor_tensor(z_sb[:, i, :], bank[UP[i]][:, 0:T], part[:, i, :], ALU.add).then_inc(z_done, 1)
                else:
                    v.tensor_tensor(z_sb[:, i, :].rearrange("p (b n) -> p b n", b=TB), hi_half,
                                    part[:, i, :].rearrange("p (b n) -> p b n", b=TB), ALU.add).then_inc(z_done, 1)
                dve.wait_ge(z_done, 2 * f + i + 1)
                v.scalar_tensor_tensor(s_sb[:, i, :], z_sb[:, i, :], 0.0, z_sb[:, i, :], ALU.max, ALU.mult
                                       ).then_inc(s_done, 1)

            def h_lo(f, par, i):
                dve.wait_ge(hhi_done, 2 * f + i + 1)
                v.tensor_tensor(hT[:, par, i, LO, :], s_sb[:, i, :], f32(hT[:, par, i, HI, :]), ALU.subtract
                                ).then_inc(hT_ready, 1)

            def step(f, par, last=False):
                for half in range(2):
                    lo_mlp(f + 1, 1 - par, 1, half)
                for i in range(2):
                    up_sum(f + 1, i)
                    if not last:
                        lo_mlp(f + 2, par, 0, i)
                    h_lo(f + 1, 1 - par, i)

            v.memset(ones[:], 1.0).then_inc(ones_made, 1)
            for tb in range(TB):
                dve.wait_ge(x_loaded[tb], 16)
                v.tensor_tensor_reduce(y_sb[:, tb, 512:D], h_sb[:, tb, 512:D], h_sb[:, tb, 512:D], 1.0, 0.0,
                                       ALU.mult, ALU.add, stat[:, tb, SS1:SS1 + 1]).then_inc(ss_early, 1)
                norm_var(0, tb, 1, (ss_early, tb + 1))
                norm_rows(tb)
                lo(0, tb, tb)
                yT_lo(0, tb)
            for half in range(2):
                lo(1, half, 2 + half)
            lo_in(0, 2, 0)
            dve.wait_ge(tables_loaded, 48)
            dve.wait_ge(bias_summed, 1)
            v.scalar_tensor_tensor(bv_sb[:], bank[BIAS][0:HEADS, 0:BV], -1.0, fill_sb[:], ALU.mult, ALU.add
                                   ).then_inc(bias_vec, 1)
            lo_in(0, 2, 1)
            lo_in(1, 0, 0)
            qk_sum(0, 2)
            lo_in(1, 0, 1)
            qk_sum(0, 3)
            lo_in(1, 1, 0)
            qk_sum(0, 4)
            lo_in(1, 1, 1)
            qk_sum(0, 5)
            with dve.Fori(1, CHUNKS_IN) as c:
                a = c - 1
                add_bias(a, 0)
                add_bias(a, 1)
                lo_in(c, 2, 0)
                sum_inverse(a, 0)
                add_bias(a, 2)
                add_bias(a, 3)
                lo_in(c, 2, 1)
                pT_copy(a, 0)
                pT_copy(a, 1)
                lo_in(c + 1, 0, 0)
                sum_inverse(a, 1)
                qk_sum(c, 2)
                out_rows_(a, 0)
                pT_copy(a, 2)
                pT_copy(a, 3)
                lo_in(c + 1, 0, 1)
                qk_sum(c, 3)
                out_rows_(a, 1)
                lo_in(c + 1, 1, 0)
                out_lo(a, 0)
                qk_sum(c, 4)
                out_lo(a, 1)
                lo_in(c + 1, 1, 1)
                qk_sum(c, 5)
            a = CHUNKS_IN - 1
            for s in range(4):
                add_bias(a, s)
                if s % 2:
                    lo(2, s // 2, 2 * (OUT0 + 2) + s // 2)
                    sum_inverse(a, s // 2)
            for s in range(4):
                pT_copy(a, s)
            for half in range(2):
                lo(3, half, 2 * (OUT0 + 3) + half)
            out_rows_(a, 0)
            out_rows_(a, 1)
            out_lo(a, 0)
            out_lo(a, 1)
            for half in range(2):
                lo_mlp(0, 0, 0, half)
            residual(0, 0, mix_done, h_done)
            residual(0, 1, mix_done, h_done)
            norm_var(1, 0, 0, (ss_early, TB + 1))
            gain_rows(1, 0)
            scale_rows(1, 0, 0)
            scale_rows(1, 0, 1)
            for half in range(2):
                lo_mlp(0, 0, 1, half)
            yT_lo(1, 0)
            residual(1, 0, mix_done, h_done)
            residual(1, 1, mix_done, h_done)
            norm_var(1, 1, 0, (ss_early, TB + 2))
            gain_rows(1, 1)
            scale_rows(1, 1, 0)
            scale_rows(1, 1, 1)
            lo_mlp(1, 1, 0, 0)
            yT_lo(1, 1)
            lo_mlp(1, 1, 0, 1)
            for i in range(2):
                up_sum(0, i, bank[UP[i]][:].rearrange("p (b l n) -> p b l n", b=TB, l=2)[:, :, HI, :])
                h_lo(0, 0, i)
            step(0, 0)
            step(1, 1)
            with dve.Fori(2, CHUNKS_UP - 2, 2) as f:
                step(f, 0)
                step(f + 1, 1)
            step(CHUNKS_UP - 2, 0, last=True)
            for tb in range(TB):
                residual(tb, 0, mlp_done, h2_done)
                residual(tb, 1, mlp_done, h2_done)
                norm_var(2, tb, 0, (ss_early, 2 * TB + tb + 1))
                gain_rows(2, tb)
                scale_rows(2, tb, 0)
                scale_rows(2, tb, 1)


_INS = ["x", "rel_bias", "norm_mix", "norm_mlp", "mlp_up", "mlp_down", "a_w_in", "a_w_out", "final_norm"]


def kernel(**inputs):
    import concourse.bacc as _bacc
    from concourse.bass_utils import run_bass_kernel_spmd as _run

    nc = _bacc.Bacc("TRN2", target_bir_lowering=False, num_devices=1)
    arrays, args = {}, []
    for name, a in [(n, np.ascontiguousarray(inputs[n])) for n in _INS] + list(shape_constants().items()):
        arrays[f"in_{name}_dram"] = a
        args.append(nc.dram_tensor(f"in_{name}_dram", a.shape, mybir.dt.from_np(a.dtype), kind="ExternalInput").ap())
    out = nc.dram_tensor("out_0_dram", (1, T, D), F32, kind="ExternalOutput").ap()
    build(nc, *args, out)
    r = _run(nc, [arrays], core_ids=[0])
    return r.results[0]["out_0_dram"]
```
